# Optimizing a Trainium2 kernel written in Bass

```python
import jax, jax.numpy as jnp
from jax import lax
import numpy as np

D_MODEL = 1024
BATCH = 1
SEQ = 1024
DEPTH = 2

N_A = DEPTH // 2
N_B = DEPTH - N_A
EPS = 1e-6

NH_A = 4
DV_A = D_MODEL // NH_A
DQK_A = DV_A // 2
CHUNK = 64
GATE_CAP = 15.0
QK_W = NH_A * DQK_A
V_W = NH_A * DV_A
IN_A = 2 * QK_W + 2 * V_W + 2 * NH_A

NH_B = 16
KVH_B = 2
GRP_B = NH_B // KVH_B
DH_B = 64
WINDOW = 128
BLK = WINDOW

D_FF = ((8 * D_MODEL // 3 + 255) // 256) * 256

kernel_name = "yoco_mlstm_swa_sink_hybrid"

def rmsnorm(x, g):
    xf = x.astype(jnp.float32)
    y = xf * lax.rsqrt(jnp.mean(xf * xf, axis=-1, keepdims=True) + EPS)
    return (y * g.astype(jnp.float32)).astype(x.dtype)

def swiglu(x, w_gate_up, w_down):
    gu = x @ w_gate_up
    g, u = jnp.split(gu, 2, axis=-1)
    return (jax.nn.silu(g) * u) @ w_down

def mlstm_chunkwise(q, k, v, ig, lf):
    Bsz, S, H, _ = q.shape
    nc = S // CHUNK

    def to_chunks(t):
        return t.reshape(Bsz, nc, CHUNK, H, -1).transpose(1, 0, 3, 2, 4)

    def gate_chunks(t):
        return t.reshape(Bsz, nc, CHUNK, H).transpose(1, 0, 3, 2)

    causal = jnp.tril(jnp.ones((CHUNK, CHUNK), dtype=bool))

    def body(carry, xs):
        C, n, m = carry
        qc, kc, vc, ic, lfc = xs
        b = jnp.cumsum(lfc, axis=-1)
        b_tot = b[..., -1]
        D = b[..., :, None] - b[..., None, :] + ic[..., None, :]
        D = jnp.where(causal, D, -jnp.inf)
        inter = b + m[..., None]
        m_t = jnp.maximum(inter, jnp.max(D, axis=-1))
        Sw = jnp.einsum('bhtd,bhsd->bhts', qc, kc) * jnp.exp(D - m_t[..., None])
        e_inter = jnp.exp(inter - m_t)
        num = jnp.einsum('bhts,bhsv->bhtv', Sw, vc) + e_inter[..., None] * jnp.einsum('bhvd,bhtd->bhtv', C, qc)
        den = jnp.sum(Sw, axis=-1) + e_inter * jnp.einsum('bhd,bhtd->bht', n, qc)
        h = num / jnp.maximum(jnp.abs(den), jnp.exp(-m_t))[..., None]
        w = b_tot[..., None] - b + ic
        m_new = jnp.maximum(b_tot + m, jnp.max(w, axis=-1))
        decay = jnp.exp(b_tot + m - m_new)
        ws = jnp.exp(w - m_new[..., None])
        C_new = decay[..., None, None] * C + jnp.einsum('bhs,bhsv,bhsd->bhvd', ws, vc, kc)
        n_new = decay[..., None] * n + jnp.einsum('bhs,bhsd->bhd', ws, kc)
        return (C_new, n_new, m_new), h

    init = (jnp.zeros((Bsz, H, v.shape[-1], q.shape[-1]), jnp.float32),
            jnp.zeros((Bsz, H, q.shape[-1]), jnp.float32),
            jnp.zeros((Bsz, H), jnp.float32))
    xs = (to_chunks(q), to_chunks(k), to_chunks(v), gate_chunks(ig), gate_chunks(lf))
    _, hs = lax.scan(body, init, xs)
    return hs.transpose(1, 0, 3, 2, 4).reshape(Bsz, S, H, -1)

def mlstm_mixer(x, w_in, b_gates, head_norm, w_out):
    Bsz, S, _ = x.shape
    proj = x @ w_in
    q, k, v, o, gates = jnp.split(proj, [QK_W, 2 * QK_W, 2 * QK_W + V_W, 2 * QK_W + 2 * V_W], axis=-1)
    gates = gates.astype(jnp.float32) + b_gates.astype(jnp.float32)
    gates = GATE_CAP * jnp.tanh(gates / GATE_CAP)
    ig, fg = jnp.split(gates, 2, axis=-1)
    lf = jax.nn.log_sigmoid(fg)
    qf = q.astype(jnp.float32).reshape(Bsz, S, NH_A, DQK_A) * (DQK_A ** -0.5)
    kf = k.astype(jnp.float32).reshape(Bsz, S, NH_A, DQK_A)
    vf = v.astype(jnp.float32).reshape(Bsz, S, NH_A, DV_A)
    h = mlstm_chunkwise(qf, kf, vf, ig, lf)
    h = h * lax.rsqrt(jnp.mean(h * h, axis=-1, keepdims=True) + EPS)
    h = h * head_norm.astype(jnp.float32).reshape(NH_A, DV_A)
    h = h.reshape(Bsz, S, V_W) * jax.nn.sigmoid(o.astype(jnp.float32))
    return h.astype(x.dtype) @ w_out

def shared_kv(x, kv_norm, w_kv, b_kv):
    Bsz, S, _ = x.shape
    nb = S // BLK
    kv = rmsnorm(x, kv_norm) @ w_kv + b_kv
    k, v = jnp.split(kv, 2, axis=-1)

    def band(t):
        tb = t.reshape(Bsz, nb, BLK, KVH_B, DH_B)
        prev = jnp.concatenate([jnp.zeros_like(tb[:, :1]), tb[:, :-1]], axis=1)
        return jnp.concatenate([prev, tb], axis=2)

    return band(k), band(v)

def swa_sink_mixer(x, k2, v2, w_q, b_q, sinks, w_out, b_out):
    Bsz, S, _ = x.shape
    nb = S // BLK
    q = (x @ w_q + b_q).reshape(Bsz, nb, BLK, KVH_B, GRP_B, DH_B)
    s = jnp.einsum('bnqkgd,bnpkd->bnkgqp', q, k2).astype(jnp.float32) * (DH_B ** -0.5)
    i = jnp.arange(BLK)[:, None]
    j = jnp.arange(2 * BLK)[None, :]
    rel = i + BLK - j
    band = (rel >= 0) & (rel < WINDOW)
    valid = band[None] & ((jnp.arange(nb) > 0)[:, None, None] | (j >= BLK)[None])
    s = jnp.where(valid[None, :, None, None], s, -jnp.inf)
    sk = sinks.astype(jnp.float32).reshape(KVH_B, GRP_B)[None, None, :, :, None, None]
    mx = jnp.maximum(jnp.max(s, axis=-1, keepdims=True), sk)
    p = jnp.exp(s - mx)
    p = p / (jnp.sum(p, axis=-1, keepdims=True) + jnp.exp(sk - mx))
    o = jnp.einsum('bnkgqp,bnpkd->bnqkgd', p.astype(v2.dtype), v2)
    return o.reshape(Bsz, S, NH_B * DH_B) @ w_out + b_out

def setup_inputs(seed: int = 0) -> dict:
    key = jax.random.key(seed)
    ks = jax.random.split(key, 24)
    f32 = jnp.float32
    nrm = lambda k, shape, scale: jax.random.normal(k, shape, f32) * scale
    b_i = nrm(ks[4], (N_A, NH_A), 0.1)
    b_f = 3.0 + nrm(ks[5], (N_A, NH_A), 0.5)
    return {
        "x": nrm(ks[0], (BATCH, SEQ, D_MODEL), 1.0),
        "a_norm": 1.0 + nrm(ks[1], (N_A, D_MODEL), 0.02),
        "a_w_in": nrm(ks[2], (N_A, D_MODEL, IN_A), D_MODEL ** -0.5),
        "a_b_gates": jnp.concatenate([b_i, b_f], axis=-1),
        "a_head_norm": 1.0 + nrm(ks[3], (N_A, V_W), 0.02),
        "a_w_out": nrm(ks[6], (N_A, V_W, D_MODEL), V_W ** -0.5),
        "kv_norm": 1.0 + nrm(ks[7], (D_MODEL,), 0.02),
        "w_kv": nrm(ks[8], (D_MODEL, 2 * KVH_B * DH_B), D_MODEL ** -0.5),
        "b_kv": nrm(ks[9], (2 * KVH_B * DH_B,), 0.02),
        "b_norm": 1.0 + nrm(ks[10], (N_B, D_MODEL), 0.02),
        "b_w_q": nrm(ks[11], (N_B, D_MODEL, NH_B * DH_B), D_MODEL ** -0.5),
        "b_b_q": nrm(ks[12], (N_B, NH_B * DH_B), 0.02),
        "b_sinks": nrm(ks[13], (N_B, NH_B), 0.5),
        "b_w_out": nrm(ks[14], (N_B, NH_B * DH_B, D_MODEL), (NH_B * DH_B) ** -0.5),
        "b_b_out": nrm(ks[15], (N_B, D_MODEL), 0.02),
        "ffn_norm": 1.0 + nrm(ks[16], (DEPTH, D_MODEL), 0.02),
        "w_gate_up": nrm(ks[17], (DEPTH, D_MODEL, 2 * D_FF), D_MODEL ** -0.5),
        "w_down": nrm(ks[18], (DEPTH, D_FF, D_MODEL), D_FF ** -0.5),
        "final_norm": 1.0 + nrm(ks[19], (D_MODEL,), 0.02),
    }

def reference(x, a_norm, a_w_in, a_b_gates, a_head_norm, a_w_out, kv_norm, w_kv, b_kv,
              b_norm, b_w_q, b_b_q, b_sinks, b_w_out, b_b_out, ffn_norm, w_gate_up, w_down, final_norm):
    k2 = v2 = None
    for l in range(DEPTH):
        if l < N_A:
            x = x + mlstm_mixer(rmsnorm(x, a_norm[l]), a_w_in[l], a_b_gates[l], a_head_norm[l], a_w_out[l])
        else:
            j = l - N_A
            x = x + swa_sink_mixer(rmsnorm(x, b_norm[j]), k2, v2, b_w_q[j], b_b_q[j], b_sinks[j], b_w_out[j], b_b_out[j])
        x = x + swiglu(rmsnorm(x, ffn_norm[l]), w_gate_up[l], w_down[l])
        if l == N_A - 1:
            k2, v2 = shared_kv(x, kv_norm, w_kv, b_kv)
    return rmsnorm(x, final_norm)


_drawn_inputs = setup_inputs


def setup_inputs(seed=0):
    import zlib

    import numpy as np

    out = dict(_drawn_inputs(seed))
    spreads = {}
    factors = {'a_head_norm': 5.13,
     'kv_norm': 8.0,
     'b_kv': 25.358,
     'b_norm': 8.0,
     'b_b_q': 8.0,
     'b_sinks': 64.0,
     'b_b_out': 26.237,
     'ffn_norm': 3.032,
     'final_norm': 8.04}
    for name, (base, spread) in spreads.items():
        noise = np.random.default_rng([zlib.crc32(name.encode()), seed]).standard_normal(out[name].shape)
        drawn = base * np.exp(spread * noise) if base else spread * noise
        out[name] = __import__('jax').numpy.asarray(drawn.astype(out[name].dtype))
    for name, factor in factors.items():
        out[name] = (out[name] * factor).astype(out[name].dtype)
    return out
```

```python
from contextlib import ExitStack

import concourse.bass as bass
from concourse import mybir

F32 = mybir.dt.float32
F32R = mybir.dt.float32r
U32 = mybir.dt.uint32
ALU = mybir.AluOpType
ACT = mybir.ActivationFunctionType
AX_X = mybir.AxisListType.X

P = 128
EPS = 1e-6
GATE_CAP = 15.0
NH_A = 4
NH_B = 16
DH_B = 64
RAW = 3
RING = 6
LEAD = 4
XS = 4
NEG = -1e30

BANK_01 = {0: 1, 1: 1}
BANK_23 = {2: 1, 3: 1}
BANK_4567 = {4: 1, 5: 1, 6: 1, 7: 1}
BANK_45 = {4: 1, 5: 1}
BANK_67 = {6: 1, 7: 1}
DOWN = {4: 4, 5: 4, 6: 4, 7: 4}
NORM = {0: 4, 1: 4, 2: 4, 3: 4}
STATE = {4: 4, 5: 4, 6: 4, 7: 3}


def add_uses(*stages):
    total = {}
    for stage in stages:
        for b, n in stage.items():
            total[b] = total.get(b, 0) + n
    return total


class BankUses:

    def __init__(self):
        self.before = [0] * 8
        self.turn = None
        self.per_turn = {}

    def so_far(self, b):
        if self.turn is None:
            return self.before[b]
        return self.before[b] + self.turn * self.per_turn[b]

    def stage(self, uses):
        base = {b: self.so_far(b) for b in uses}
        for b, n in uses.items():
            self.before[b] += n
        return base

    def enter_loop(self, turn, per_turn):
        self.turn, self.per_turn, self.at_entry = turn, per_turn, list(self.before)

    def leave_loop(self, turns):
        for b in range(8):
            assert self.before[b] - self.at_entry[b] == self.per_turn.get(b, 0)
            self.before[b] += self.per_turn.get(b, 0) * (turns - 1)
        self.turn = None


class Unit:

    def __init__(self, base, turn=0):
        if isinstance(turn, int):
            base, turn = base + RING * turn, 0
        self.base, self.turn = base, turn
        self.n = base + RING * turn
        self.slot = base % RING
        self.raw = base % RAW
        self.in_loop = not isinstance(turn, int)

    def __add__(self, k):
        return Unit(self.base + k, self.turn)


def yoco_kernel(nc, x, a_norm, a_w_in, a_b_gates, a_head_norm, a_w_out, kv_norm, w_kv, b_kv,
                b_norm, b_w_q, b_b_q, b_sinks, b_w_out, b_b_out, ffn_norm, w_gate_up, w_down,
                final_norm, out):
    _, S, D = x.shape
    KT = D // P
    TT = S // P
    FF = w_down.shape[1]
    FT = FF // P
    FP = FT // 2
    DV = D // NH_A
    DQK = DV // 2
    assert S == 1024 and D == 1024 and DQK == P and FT % 2 == 0 and TT == 8 and KT == 8
    QK_SCALE = float(DQK) ** -0.5
    ATT_SCALE = float(DH_B) ** -0.5
    PAIRS = NH_B // 2
    STEPS = PAIRS * TT

    U_GATES = 0
    U_HEADS = 1
    U_AOUT = U_HEADS + 6 * NH_A
    U_FFN = [U_AOUT + KT, 0]
    U_KV = U_FFN[0] + 3 * FT
    U_Q = U_KV + 2
    U_BOUT = U_Q + PAIRS
    U_FFN[1] = U_BOUT + KT
    UNITS = U_FFN[1] + 3 * FT

    dmas_of = [0 if u == U_GATES else 2 if U_Q <= u < U_FFN[1] else 1 for u in range(UNITS)]
    arrived_at = [16 * sum(dmas_of[v] for v in range(u % RAW, u + 1, RAW)) for u in range(UNITS)]

    gain_of = [None] * UNITS
    for u in range(U_AOUT):
        gain_of[u] = 0
    for u in range(U_KV, U_Q):
        gain_of[u] = 1
    for u in range(U_Q, U_BOUT):
        gain_of[u] = 2
    for l in range(2):
        for u in range(3 * FT - 2):
            if u < 4 or (u - 4) % RING not in (1, 2):
                gain_of[U_FFN[l] + u] = 3 + l
    gained_up_to = [sum(g is not None for g in gain_of[:u + 1]) for u in range(UNITS)]
    gained_per_turn = {0: 6, 3: 4, 4: 4}

    x2 = x[0]
    out2 = out[0]
    win = a_w_in[0].rearrange("(k p) n -> p k n", p=P)
    awo = a_w_out[0]
    wkv = w_kv.rearrange("(k p) n -> p k n", p=P)
    wq = b_w_q[0].rearrange("(k p) (a u d) -> p k u a d", p=P, a=2, d=DH_B)
    bwo = b_w_out[0]
    wgu = [w_gate_up[l].rearrange("(k p) n -> p k n", p=P) for l in range(2)]
    wdn = [w_down[l] for l in range(2)]

    scr_negm = nc.dram_tensor("scratch_neg_m", (NH_A, S), F32, kind="Internal").ap()
    scr_einter = nc.dram_tensor("scratch_e_inter", (NH_A, S), F32, kind="Internal").ap()
    scr_decay = nc.dram_tensor("scratch_decay", (NH_A, TT), F32, kind="Internal").ap()

    with ExitStack() as ctx:
        base = (nc.sbuf_base + 31) // 32 * 32
        KB = 1024
        TILE = 4 * KB
        o_xh, o_xl = base, base + 8 * TILE
        o_raw = o_xl + 8 * TILE
        o_wh = o_raw + RAW * TILE
        o_wl = o_wh + RING * TILE
        o_X = o_wl + RING * TILE
        o_R = o_X + 8 * TILE
        o_T = o_R + 8 * TILE
        o_C = o_T + 4 * TILE

        def at(name, shape, off, dt=F32):
            return nc.alloc_sbuf_tensor_at(name, shape, dt, offset=off)

        xh = at("xT_hi", [P, KT, S], o_xh, F32R)
        xl = at("xT_lo", [P, KT, S], o_xl, F32R)
        raw = at("raw", [P, RAW, 1024], o_raw)
        wh = at("w_hi", [P, RING, 1024], o_wh, F32R)
        wl = at("w_lo", [P, RING, 1024], o_wl, F32R)
        X = at("X", [P, TT, D], o_X)
        yT = at("yT", [P, KT, S], o_R)
        sg = at("silu_gate", [P, S], o_R)
        hf = at("hidden", [P, S], o_R + TILE)
        gain_row = at("gain_row", [P, D], o_R + 2 * TILE)
        bout = at("b_out_row", [P, D], o_R + 2 * TILE)
        junk = at("squares", [P, D], o_R + 3 * TILE)
        xs = at("x_normed", [P, XS, D], o_R + 4 * TILE)
        hh = at("hidden_hi", [P, 2, S], o_T, F32R)
        hl = at("hidden_lo", [P, 2, S], o_T + 2 * TILE, F32R)
        ig = at("gate_i", [NH_A, S], o_R)
        fg = at("gate_f", [NH_A, S], o_R + TILE)
        enf = at("exp_neg_f", [NH_A, S], o_R + 2 * TILE)
        one_enf = at("one_plus_exp", [NH_A, S], o_R + 3 * TILE)
        lnu = at("ln_one_plus", [NH_A, S], o_R + 4 * TILE)
        lf = at("log_forget", [NH_A, S], o_R + 5 * TILE)
        mrow = at("m_row", [NH_A, S], o_R + 6 * TILE)
        brow = at("b_row", [NH_A, S], o_R + 7 * TILE)
        qT = at("qT", [P, S], o_X)
        kT = at("kT", [P, S], o_X + TILE)
        W1 = 256 + 1
        v1 = at("v_one", [P, TT, W1], o_X + 2 * TILE)
        o = o_X + 2 * TILE + (TT * W1 * 4 + 31) // 32 * 32
        SwT = at("SwT", [P, TT, P], o)
        kw = at("k_weighted", [P, TT, DQK], o + TILE)
        C = at("C_state", [P, 2, W1 + 7], o + 2 * TILE)
        assert o + 2 * TILE + 2 * (W1 + 7) * 4 <= o_R
        H = at("h_head", [P, TT, DV], o_T)
        qe = at("q_e_inter", [P, S], o_T + 2 * TILE)
        cols = at("gate_cols", [P, TT, 3, NH_A], o_T + 3 * TILE)
        decay = at("decay", [P, NH_A * TT], o_T + 3 * TILE + 512)
        hsq = at("h_sumsq", [P, 3, TT], o_T + 3 * TILE + 1024)
        dn = at("den", [P, TT, 3], o_T + 3 * TILE + 1280)
        hjunk = at("h_squares", [P, DV], o_T + 3 * TILE + 2048)
        G = at("gate_stack", [P, S], o_T)
        negm = at("neg_M", [NH_A, S], o_T + TILE)
        einter = at("e_inter", [NH_A, S], o_T + 2 * TILE)
        chunk_mask = at("chunk_mask", [NH_A, S], o)
        diff = at("diff_row", [NH_A, S], o + TILE)
        kTb = at("kT_b", [P, S], o_T)
        vb = at("v_b", [P, TT, P], o_T + TILE)
        Sm = at("S_merged", [P, 2, 2, P], o_T + 2 * TILE)
        Pr = at("probs", [P, 2, 2, P], o_T + 2 * TILE + 2048)
        PTc = at("probsT_cur", [P, 2, P], o_T + 3 * TILE)
        PTp = at("probsT_prev", [P, 2, P], o_T + 3 * TILE + 1024)
        on = at("o_block", [P, P], o_T + 3 * TILE + 2048)
        st = at("softmax_cols", [P, 4, 6, 2], o_T + 3 * TILE + 2560)
        vT = at("vT_b", [P, S], o_R + 7 * TILE)

        off = [o_C]

        def const(name, shape, dt=F32):
            n = 4
            for s in shape[1:]:
                n *= s
            t = at(name, shape, off[0], dt)
            off[0] += (n + 31) // 32 * 32
            assert off[0] <= nc.sbuf_usable_end
            return t

        ident = const("ident", [P, P])
        mask_neg = const("mask_neg", [P, P])
        keep_le = const("keep_le", [P, P])
        keepT_cur = const("keepT_cur", [P, P])
        keepT_prev = const("keepT_prev", [P, P])
        neghalf = const("neghalf", [P, TT])
        ssq = const("ssq", [P, TT])
        ms = const("ms", [P, TT])
        rstd = const("rstd", [P, TT])
        hn = const("head_norm", [P, KT])
        bgate = const("b_gates", [P, 2])
        mprev = const("m_prev", [NH_A, 3, TT])
        gcol = const("gain_cols", [P, 5, KT])
        bkv = const("b_kv", [P, 2])
        bq = const("b_q", [P, 2, PAIRS])
        sink = const("sinks", [P, 2, NH_B])

        ps = ctx.enter_context(nc.psum_tensor("ps", [P, 8, 512], F32))

        def sem(name):
            return ctx.enter_context(nc.semaphore(name))

        raw_loaded = [sem(f"raw_loaded{r}") for r in range(RAW)]
        gate_w_cleared, gate_w_loaded = sem("gate_w_cleared"), sem("gate_w_loaded")
        unit_gained = sem("unit_gained")
        hi_ready, lo_ready = sem("hi_ready"), sem("lo_ready")
        unit_begun = sem("unit_begun")
        bank_full = [sem(f"bank_full{b}") for b in range(8)]
        bank_free = [sem(f"bank_free{b}") for b in range(8)]
        x_loaded = [sem(f"x_loaded{t}") for t in range(TT)]
        gain_loaded = sem("gain_loaded")
        a_gain_loaded, gains_loaded, bgate_loaded = sem("a_gain_loaded"), sem("gains_loaded"), sem("bgate_loaded")
        consts_loaded, consts_set, const_step = sem("consts_loaded"), sem("consts_set"), sem("const_step")
        ssq_ready, ms_ready, rstd_ready = sem("ssq_ready"), sem("ms_ready"), sem("rstd_ready")
        xs_ready, xt_hi_ready = sem("xs_ready"), sem("xt_hi_ready")
        hh_ready, h_ready = sem("hh_ready"), sem("h_ready")
        gate_act, gate_dve = sem("gate_act"), sem("gate_dve")
        rows_stored, decay_loaded = sem("rows_stored"), sem("decay_loaded")
        neg_loaded, ein_loaded = sem("neg_loaded"), sem("ein_loaded")
        qe_ready, D_ready, Dm_ready, E_ready = (
            sem("qe_ready"), sem("D_ready"), sem("Dm_ready"), sem("E_ready"))
        den_step, den_ready, num_ready, C_ready = (
            sem("den_step"), sem("den_ready"), sem("num_ready"), sem("C_ready"))
        hms_ready, hrs_ready, H_ready = (
            sem("hms_ready"), sem("hrs_ready"), sem("H_ready"))
        y_hi_ready, y_ready = sem("y_hi_ready"), sem("y_ready")
        bq_scaled = sem("bq_scaled")
        bout_loaded, bout_added = sem("bout_loaded"), sem("bout_added")
        scores_ready, probsT_ready, o_ready, oT_ready = (
            sem("scores_ready"), sem("probsT_ready"), sem("o_ready"), sem("oT_ready"))
        blank_set, prev_copied, merged, rowmax_ready, negmax_ready, sinkarg_ready = (
            sem("blank_set"), sem("prev_copied"), sem("merged"), sem("rowmax_ready"), sem("negmax_ready"), sem("sinkarg_ready"))
        probs_ready, den_sum, rcp_ready, pt_ready, on_ready, oT_copied = (
            sem("probs_ready"), sem("den_sum"), sem("rcp_ready"), sem("pt_ready"), sem("on_ready"), sem("oT_copied"))
        out_stored = [sem(f"out_stored{i}") for i in range(XS)]

        ds = bass.ds
        HEAD_USES = add_uses(BANK_01, BANK_4567, BANK_23, BANK_4567, BANK_01, BANK_23, BANK_4567,
                             BANK_01, BANK_23, STATE)
        FFN_USES = add_uses(BANK_01, DOWN, BANK_23, BANK_01, BANK_23)

        output_pieces = [(t, slice(0, D)) for t in range(TT - 1)] + [
            (TT - 1, slice(0, D // 2)), (TT - 1, slice(D // 2, D))]

        def raw_arrivals(u):
            return arrived_at[u.base] + 16 * (RING // RAW) * u.turn

        block = ctx.enter_context(nc.Block())

        @block.sync
        def _(sp):
            def raw_is_free(u):
                if u.in_loop or u.n >= RAW:
                    sp.wait_ge(lo_ready, u.n - RAW + 1)

            def load_cols(u, src):
                raw_is_free(u)
                sp.dma_start(raw[:, u.raw, :].rearrange("p (k n) -> p k n", k=KT), src
                             ).then_inc(raw_loaded[u.raw], 16)

            def load_rows(u, src):
                raw_is_free(u)
                sp.dma_start(raw[:, u.raw, :], src).then_inc(raw_loaded[u.raw], 16)

            def load_head(h, turn, units=range(6)):
                first = [h * DQK, NH_A * DQK + h * DQK, 2 * NH_A * DQK + h * DV, 2 * NH_A * DQK + h * DV + P,
                         2 * NH_A * DQK + D + h * DV, 2 * NH_A * DQK + D + h * DV + P]
                for j in units:
                    load_cols(Unit(U_HEADS + j, turn), win[:, :, ds(first[j], P)])

            def load_x(t):
                sp.dma_start(X[:, t, :], x2[t * P:(t + 1) * P, :]).then_inc(x_loaded[t], 16)

            def load_gains(i, g):
                sp.dma_start(gcol[:, i, :], g.rearrange("(k p) -> p k", p=P), allow_slow_non_contiguous=True
                             ).then_inc(a_gain_loaded if i == 0 else gains_loaded, 16)

            for t in range(3):
                load_x(t)
            sp.wait_ge(gate_w_cleared, 1)
            gates = raw[:, 0, :].rearrange("p (k n) -> p k n", k=KT)
            g0 = 2 * NH_A * DQK + 2 * D
            sp.dma_start(gates[:, :, 0:NH_A], win[:, :, g0:g0 + NH_A]).then_inc(gate_w_loaded, 16)
            sp.dma_start(gates[:, :, 32:32 + NH_A], win[:, :, g0 + NH_A:g0 + 2 * NH_A]).then_inc(gate_w_loaded, 16)
            load_gains(0, a_norm[0, :])
            for t in range(3, TT):
                load_x(t)
            load_head(0, 0, range(2))
            sp.dma_start(bgate[0:NH_A, 0:1], a_b_gates[0, 0:NH_A].unsqueeze(1)).then_inc(bgate_loaded, 16)
            sp.dma_start(bgate[32:32 + NH_A, 0:1], a_b_gates[0, NH_A:2 * NH_A].unsqueeze(1)
                         ).then_inc(bgate_loaded, 16)
            load_head(0, 0, range(2, 6))
            sp.dma_start(hn[:], a_head_norm[0, :].rearrange("(k p) -> p k", p=P),
                         allow_slow_non_contiguous=True).then_inc(consts_loaded, 16)
            load_gains(1, kv_norm)
            load_gains(2, b_norm[0, :])
            sp.dma_start(gcol[:, 3:5, :], ffn_norm.rearrange("l (k p) -> p l k", p=P),
                         allow_slow_non_contiguous=True).then_inc(gains_loaded, 16)
            sp.dma_start(bkv[:], b_kv.rearrange("(k p) -> p k", p=P),
                         allow_slow_non_contiguous=True).then_inc(consts_loaded, 16)
            for a in range(2):
                sp.dma_start(bq[a * DH_B:(a + 1) * DH_B, 0, :],
                             b_b_q[0, a * 512:(a + 1) * 512].rearrange("(u d) -> d u", d=DH_B),
                             allow_slow_non_contiguous=True).then_inc(consts_loaded, 16)
            sp.dma_start(sink[:, 0, :], b_sinks[0, :].partition_broadcast(P)).then_inc(consts_loaded, 16)
            with sp.Fori(1, NH_A) as h:
                load_head(h, h)
            for k in range(KT):
                load_rows(Unit(U_AOUT + k), awo[k * P:(k + 1) * P, :])

            def load_ffn(l):
                u0 = U_FFN[l]
                load_cols(Unit(u0), wgu[l][:, :, 0:P])
                load_cols(Unit(u0 + 1), wgu[l][:, :, FF:FF + P])
                load_cols(Unit(u0 + 2), wgu[l][:, :, P:2 * P])
                load_cols(Unit(u0 + 3), wgu[l][:, :, FF + P:FF + 2 * P])
                with sp.Fori(1, FP) as i:
                    t = i - 1
                    load_cols(Unit(u0 + 4, t), wgu[l][:, :, ds(i * (2 * P), P)])
                    load_rows(Unit(u0 + 5, t), wdn[l][ds(t * (2 * P), P), :])
                    load_rows(Unit(u0 + 6, t), wdn[l][ds(t * (2 * P) + P, P), :])
                    load_cols(Unit(u0 + 7, t), wgu[l][:, :, ds(i * (2 * P) + FF, P)])
                    load_cols(Unit(u0 + 8, t), wgu[l][:, :, ds(i * (2 * P) + P, P)])
                    load_cols(Unit(u0 + 9, t), wgu[l][:, :, ds(i * (2 * P) + FF + P, P)])
                for j in range(2):
                    load_rows(Unit(u0 + 3 * FT - 2 + j), wdn[l][FF - (2 - j) * P:FF - (1 - j) * P, :])

            load_ffn(0)
            load_cols(Unit(U_KV), wkv[:, :, 0:P])
            load_cols(Unit(U_KV + 1), wkv[:, :, P:2 * P])
            for u in range(PAIRS):
                un = Unit(U_Q + u)
                raw_is_free(un)
                dst = raw[:, un.raw, :].rearrange("p (k a d) -> p k a d", k=KT, a=2)
                for a in range(2):
                    sp.dma_start(dst[:, :, a], wq[:, :, u, a]).then_inc(raw_loaded[un.raw], 16)
            for u in range(PAIRS):
                un = Unit(U_BOUT + u)
                raw_is_free(un)
                for a in range(2):
                    r0 = (a * PAIRS + u) * DH_B
                    sp.dma_start(raw[a * DH_B:(a + 1) * DH_B, un.raw, :], bwo[r0:r0 + DH_B, :]
                                 ).then_inc(raw_loaded[un.raw], 16)
            load_ffn(1)
            stores = [0] * XS
            for n, (t, c) in enumerate(output_pieces):
                sp.wait_ge(xs_ready, 4 * TT + n + 1)
                sp.dma_start(out2[t * P:(t + 1) * P, c], xs[:, t % XS, c]).then_inc(out_stored[t % XS], 16)
                stores[t % XS] += 1
            for i in range(XS):
                sp.wait_ge(out_stored[i], 16 * stores[i])

        @block.gpsimd
        def _(pool):
            pool.memset(raw[:, 0, :], 0.0).then_inc(gate_w_cleared, 1)
            pool.memset(neghalf[:], -0.5).then_inc(const_step, 1)
            pool.memset(ident[:], 0.0).then_inc(const_step, 1)
            pool.memset(mask_neg[:], 0.0).then_inc(const_step, 1)
            for t in (keep_le, keepT_cur, keepT_prev):
                pool.memset(t[:], 1.0).then_inc(const_step, 1)
            pool.wait_ge(const_step, 6)
            row, col = [[1, P]], [[-1, P]]
            pool.affine_select(out=ident[:], in_=ident[:], compare_op=ALU.not_equal, fill=1.0, base=0,
                               pattern=col, channel_multiplier=1).then_inc(consts_set, 1)
            pool.affine_select(out=mask_neg[:], in_=mask_neg[:], compare_op=ALU.is_ge, fill=NEG, base=0,
                               pattern=row, channel_multiplier=-1).then_inc(consts_set, 1)
            pool.affine_select(out=keep_le[:], in_=keep_le[:], compare_op=ALU.is_ge, fill=0.0, base=0,
                               pattern=col, channel_multiplier=1).then_inc(consts_set, 1)
            pool.affine_select(out=keepT_cur[:], in_=keepT_cur[:], compare_op=ALU.is_ge, fill=0.0, base=0,
                               pattern=row, channel_multiplier=-1).then_inc(consts_set, 1)
            pool.affine_select(out=keepT_prev[:], in_=keepT_prev[:], compare_op=ALU.is_ge, fill=0.0, base=-1,
                               pattern=col, channel_multiplier=1).then_inc(consts_set, 1)

            def rstd_of_tiles(norm, tiles=range(TT)):
                for t in tiles:
                    pool.wait_ge(ms_ready, norm * TT + t + 1)
                    pool.tensor_tensor(rstd[:, t:t + 1], ms[:, t:t + 1], neghalf[:, t:t + 1], ALU.pow
                                       ).then_inc(rstd_ready, 1)

            def gain(u):
                if u.base == U_GATES:
                    pool.wait_ge(gate_w_loaded, 32)
                    pool.wait_ge(a_gain_loaded, 16)
                else:
                    pool.wait_ge(raw_loaded[u.raw], raw_arrivals(u))
                v = raw[:, u.raw, :].rearrange("p (k n) -> p k n", k=KT)
                g = gcol[:, gain_of[u.base], :].unsqueeze(2).to_broadcast([P, KT, P])
                pool.tensor_tensor(v, v, g, ALU.mult).then_inc(unit_gained, 1)

            def gain_of_ffn(l):
                u0 = U_FFN[l]
                gain(Unit(u0 + 4))
                gain(Unit(u0 + 7))
                with pool.Fori(1, FP - 1) as i:
                    for j in (8, 9, 4 + RING, 7 + RING):
                        gain(Unit(u0 + j, i - 1))
                for j in (8, 9):
                    gain(Unit(u0 + j, FP - 2))

            def y_lo(n0, k):
                pool.wait_ge(y_hi_ready, n0 * KT + k + 1)
                hi = xh[:, k, :] if k < 6 else hh[:, k - 6, :]
                lo = xl[:, k, :] if k < 6 else hl[:, k - 6, :]
                pool.tensor_tensor(lo, yT[:, k, :], hi.bitcast(F32), ALU.subtract).then_inc(y_ready, 1)

            rstd_of_tiles(0, range(4))
            gain(Unit(U_GATES))
            rstd_of_tiles(0, range(4, TT))
            for j in range(3):
                gain(Unit(U_HEADS + j))

            pool.wait_ge(xs_ready, TT)
            pool.memset(v1[:, :, 256:257], 1.0).then_inc(const_step, 1)
            pool.memset(chunk_mask[:], 1.0).then_inc(const_step, 1)
            pool.memset(G[:], 0.0).then_inc(const_step, 1)
            pool.memset(mprev[:], 0.0).then_inc(const_step, 1)
            pool.wait_ge(const_step, 10)
            pool.memset(chunk_mask[:].rearrange("h (c t) -> h c t", t=P)[:, :, 0:1], 0.0).then_inc(const_step, 1)

            for j in range(3, 6):
                gain(Unit(U_HEADS + j))

            pool.wait_ge(gate_dve, 10)
            pool.dma_start(scr_negm, negm[:]).then_inc(rows_stored, 16)
            pool.wait_ge(gate_act, 7)
            pool.dma_start(scr_einter, einter[:]).then_inc(rows_stored, 16)
            pool.dma_start(scr_decay, mprev[:, 2, :]).then_inc(rows_stored, 16)
            pool.wait_ge(rows_stored, 48)
            pool.wait_ge(gate_dve, 12)
            pool.dma_start(decay[:], scr_decay.rearrange("h c -> (h c)").partition_broadcast(P)
                           ).then_inc(decay_loaded, 16)

            def load_rows_of_head(h):
                pool.dma_start(SwT[:].rearrange("p c t -> p (c t)"),
                               scr_negm[ds(h, 1), :].rearrange("a n -> (a n)").partition_broadcast(P)
                               ).then_inc(neg_loaded, 16)
                pool.dma_start(qe[:], scr_einter[ds(h, 1), :].rearrange("a n -> (a n)").partition_broadcast(P)
                               ).then_inc(ein_loaded, 16)

            def rstd_of_head(h):
                pool.wait_ge(hms_ready, h + 1)
                pool.tensor_tensor(hsq[:, 2, :], hsq[:, 1, :], neghalf[:], ALU.pow).then_inc(hrs_ready, 1)

            load_rows_of_head(0)
            for j in range(6, 11):
                gain(Unit(U_HEADS + j))
            with pool.Fori(1, NH_A - 1) as h:
                pool.wait_ge(num_ready, h * TT)
                load_rows_of_head(h)
                rstd_of_head(h - 1)
                for j in range(LEAD + 1, LEAD + 1 + RING):
                    gain(Unit(U_HEADS + j, h))
            pool.wait_ge(num_ready, (NH_A - 1) * TT)
            load_rows_of_head(NH_A - 1)
            rstd_of_head(NH_A - 2)
            gain(Unit(U_HEADS + 5, NH_A - 1))

            for k in (0, 1):
                y_lo(0, k)
            rstd_of_head(NH_A - 1)
            for k in range(2, KT):
                y_lo(0, k)
            pool.wait_ge(gains_loaded, 16 * 3)
            for j in range(4):
                gain(Unit(U_FFN[0] + j))
            rstd_of_tiles(1)
            gain_of_ffn(0)

            pool.wait_ge(y_ready, KT)
            pool.dma_start(bout[:], b_b_out[0, :].partition_broadcast(P)).then_inc(bout_loaded, 16)
            for j in range(2 + PAIRS):
                if j == LEAD:
                    rstd_of_tiles(2)
                gain(Unit(U_KV + j))
                if j == LEAD + 1:
                    pool.wait_ge(bout_loaded, 16)
                    pool.wait_ge(xs_ready, 3 * TT)
                    for t in range(TT):
                        pool.tensor_tensor(X[:, t, :], X[:, t, :], bout[:], ALU.add).then_inc(bout_added, 1)
            for k in range(KT):
                y_lo(1, k)
            pool.wait_ge(y_ready, 2 * KT)
            pool.dma_start(gain_row[:], final_norm.partition_broadcast(P)).then_inc(gain_loaded, 16)
            for j in range(4):
                gain(Unit(U_FFN[1] + j))
            rstd_of_tiles(3)
            gain_of_ffn(1)
            rstd_of_tiles(4)

        @block.scalar
        def _(act):
            uses = BankUses()

            def write_hi(u):
                if u.base >= UNITS:
                    return
                if gain_of[u.base] is not None:
                    act.wait_ge(unit_gained, gained_up_to[u.base] + gained_per_turn.get(gain_of[u.base], 0) * u.turn)
                else:
                    act.wait_ge(raw_loaded[u.raw], raw_arrivals(u))
                if u.in_loop or u.n >= RING:
                    act.wait_ge(unit_begun, u.n - RING + 2)
                act.activation(wh[:, u.slot, :], raw[:, u.raw, :], ACT.Copy).then_inc(hi_ready, 1)

            def square(norm, t):
                if norm * TT + t:
                    act.wait_ge(ssq_ready, norm * TT + t)
                act.activation(junk[:], X[:, t, :], ACT.Square, accum_out=ssq[:, t:t + 1]).then_inc(ssq_ready, 1)

            def xt_hi(K, t):
                for j in range(2):
                    b = 2 * (t % 2) + j
                    act.wait_ge(bank_full[b], K[b] + t // 2 + 1)
                    act.activation(xh[:, 4 * j:4 * j + 4, t * P:(t + 1) * P],
                                   ps[:, b, :].rearrange("p (k n) -> p k n", k=4), ACT.Copy
                                   ).then_inc(xt_hi_ready, 1)

            def down_and_norm(pair, norm, last=False):
                write_hi(pair + LEAD)
                write_hi(pair + (LEAD + 1))
                Kd = uses.stage(DOWN)
                Kn = None if last else uses.stage(NORM)
                for t in range(TT + 3):
                    if t >= 3 and not last:
                        xt_hi(Kn, t - 3)
                    if t < TT:
                        g = 2 * t + 1
                        act.wait_ge(bank_free[4 + g % 4], Kd[4 + g % 4] + g // 4 + 1)
                        square(norm, t)

            K = uses.stage(NORM)
            for t in range(TT + 2):
                if t < TT:
                    act.wait_ge(x_loaded[t], 16)
                    square(0, t)
                if t >= 2:
                    xt_hi(K, t - 2)
                if t == 5:
                    write_hi(Unit(U_GATES))
                if t >= TT:
                    write_hi(Unit(U_HEADS + t - TT))

            K = uses.stage(BANK_45)
            act.wait_ge(gate_dve, 1)
            for half in range(2):
                c = slice(half * 512, (half + 1) * 512)
                b = 4 + half
                act.wait_ge(bank_full[b], K[b] + 1)
                act.activation(ig[:, c], ps[0:NH_A, b, :], ACT.Tanh, scale=1.0 / GATE_CAP,
                               bias=bgate[0:NH_A, 1:2])
                act.activation(fg[:, c], ps[32:32 + NH_A, b, :], ACT.Tanh, scale=1.0 / GATE_CAP,
                               bias=bgate[32:32 + NH_A, 1:2]).then_inc(bank_free[b], 1)
                if half == 0:
                    write_hi(Unit(U_HEADS + 2))
            act.wait_ge(bank_free[5], K[5] + 1)
            act.activation(enf[:], fg[:], ACT.Exp, scale=-GATE_CAP).then_inc(gate_act, 1)
            act.wait_ge(gate_dve, 3)
            act.activation(lnu[:], one_enf[:], ACT.Ln).then_inc(gate_act, 1)
            act.wait_ge(gate_act, 2)
            act.activation(fg[:], lnu[:], ACT.Exp, scale=-1.0).then_inc(gate_act, 1)
            act.wait_ge(gate_dve, 8)
            act.activation(G[32:32 + NH_A, :], mrow[:], ACT.Exp, scale=-1.0).then_inc(gate_act, 1)
            act.wait_ge(gate_dve, 12)
            act.activation(G[64:64 + NH_A, :], brow[:], ACT.Exp).then_inc(gate_act, 1)
            act.activation(einter[:], diff[:], ACT.Exp).then_inc(gate_act, 1)
            act.activation(mprev[:, 2, :], mprev[:, 1, :], ACT.Exp).then_inc(gate_act, 1)
            write_hi(Unit(U_HEADS + 3))

            def head(h, turn, first, last=False):
                un = [Unit(U_HEADS + j, turn) for j in range(6)]
                write_hi(un[0] + LEAD)
                K = uses.stage(BANK_01)
                for half in range(2):
                    act.wait_ge(bank_full[half], K[half] + 1)
                    act.activation(qT[:, half * 512:(half + 1) * 512], ps[:, half, :], ACT.Copy, scale=QK_SCALE
                                   ).then_inc(bank_free[half], 1)
                if not first:
                    uses.stage(BANK_4567)
                write_hi(un[1] + LEAD)
                K = uses.stage(BANK_23)
                for half in range(2):
                    act.wait_ge(bank_full[2 + half], K[2 + half] + 1)
                    act.activation(kT[:, half * 512:(half + 1) * 512], ps[:, 2 + half, :], ACT.Copy
                                   ).then_inc(bank_free[2 + half], 1)
                write_hi(un[2] + LEAD)
                write_hi(un[3] + LEAD)

                def v_tiles(t0):
                    K = uses.stage(BANK_4567)
                    for t in range(t0, t0 + 4):
                        b = 4 + t % 4
                        act.wait_ge(bank_full[b], K[b] + 1)
                        act.activation(v1[:, t, 0:DV], ps[:, b, 0:DV], ACT.Copy).then_inc(bank_free[b], 1)

                v_tiles(0)
                if first:
                    uses.stage(BANK_67)
                uses.stage(BANK_01)
                uses.stage(BANK_23)
                act.wait_ge(Dm_ready, h + 1)
                flat = SwT[:].rearrange("p c t -> p (c t)")
                act.activation(flat, flat, ACT.Exp).then_inc(E_ready, 1)
                v_tiles(4)
                Ko = [uses.stage(BANK_01), uses.stage(BANK_23)]
                Ks = uses.stage(STATE)
                for c in range(TT):
                    if c % 4 == 0:
                        write_hi(un[4 + c // 4] + LEAD)
                    i = 2 * c
                    b = 4 + i % 4
                    act.wait_ge(den_ready, h * TT + c + 1)
                    act.activation(H[:, c, :], ps[:, b, 0:DV], ACT.Copy, scale=dn[:, c, 2:3]
                                   ).then_inc(bank_free[b], 1)
                    act.wait_ge(bank_free[b], Ks[b] + i // 4 + 1)
                    act.activation(hjunk[:], H[:, c, :], ACT.Square, accum_out=hsq[:, 0, c:c + 1]
                                   ).then_inc(num_ready, 1)
                    act.wait_ge(num_ready, h * TT + c + 1)
                    if last and c >= 5:
                        y_hi(2 * c - 10)
                        y_hi(2 * c - 9)
                    if c % 4 == 3:
                        j = c // 4
                        for half in range(2):
                            b_o = 2 * j + half
                            act.wait_ge(bank_full[b_o], Ko[j][b_o] + 1)
                            act.activation(yT[:, ds(2 * h + j, 1), half * 512:(half + 1) * 512],
                                           ps[:, b_o, :].unsqueeze(1), ACT.Sigmoid).then_inc(bank_free[b_o], 1)

            def y_hi(k):
                dst = xh[:, k, :] if k < 6 else hh[:, k - 6, :]
                act.activation(dst, yT[:, k, :], ACT.Copy).then_inc(y_hi_ready, 1)

            head(0, 0, True)
            with act.Fori(1, NH_A - 1) as h:
                uses.enter_loop(h - 1, HEAD_USES)
                head(h, h, False)
            uses.leave_loop(NH_A - 2)
            head(NH_A - 1, NH_A - 1, False, last=True)

            for t in range(TT):
                act.dma_start(X[:, t, :], x2[t * P:(t + 1) * P, :]).then_inc(x_loaded[t], 16)
            for j in range(3):
                write_hi(Unit(U_AOUT + 2 * j) + LEAD)
                write_hi(Unit(U_AOUT + 2 * j + 1) + LEAD)
                uses.stage(DOWN)
                if j == 0:
                    K = uses.stage(BANK_4567)
                    act.wait_ge(bank_free[7], K[7] + 1)
                    for k in (6, 7):
                        y_hi(k)
            down_and_norm(Unit(U_AOUT + 6), 1)

            def silu(b0=0):
                K = uses.stage({b0: 1, b0 + 1: 1})
                for half in range(2):
                    b = b0 + half
                    act.wait_ge(bank_full[b], K[b] + 1)
                    act.wait_ge(bank_free[2 + half], uses.so_far(2 + half))
                    act.activation(sg[:, half * 512:(half + 1) * 512], ps[:, b, :], ACT.Silu
                                   ).then_inc(bank_free[b], 1)

            def hidden_hi(j):
                K = uses.stage(BANK_23)
                for half in range(2):
                    act.wait_ge(bank_free[2 + half], K[2 + half] + 1)
                    act.activation(hh[:, j, half * 512:(half + 1) * 512],
                                   hf[:, half * 512:(half + 1) * 512], ACT.Copy).then_inc(hh_ready, 1)

            def ffn(l, norm_after):
                u0, t0 = U_FFN[l], l * FT
                for j in range(2):
                    write_hi(Unit(u0 + 2 * j) + LEAD)
                    silu(0 if j else 4)
                    write_hi(Unit(u0 + 2 * j + 1) + LEAD)
                    hidden_hi(j)

                def pair(i, un):
                    write_hi(un + LEAD)
                    write_hi(un + (1 + LEAD))
                    silu()
                    write_hi(un + (2 + LEAD))
                    uses.stage(DOWN)
                    write_hi(un + (3 + LEAD))
                    hidden_hi(0)
                    write_hi(un + (4 + LEAD))
                    silu()
                    write_hi(un + (5 + LEAD))
                    hidden_hi(1)

                with act.Fori(1, FP - 1) as i:
                    uses.enter_loop(i - 1, FFN_USES)
                    pair(i, Unit(u0 + 4, i - 1))
                uses.leave_loop(FP - 2)
                pair(FP - 1, Unit(u0 + 4 + RING * (FP - 2)))
                down_and_norm(Unit(u0 + 3 * FT - 2), norm_after, last=(l == 1))

            ffn(0, 2)

            for j in range(2):
                write_hi(Unit(U_KV + j) + LEAD)
            uses.stage(BANK_45)
            uses.stage(BANK_23)
            def query_out(u, K, k):
                for half in range(2):
                    act.wait_ge(bank_full[half], K[half] + k + 1)
                    if half == 0 and u == 2:
                        act.wait_ge(bout_added, TT)
                    act.activation(yT[:, u, half * 512:(half + 1) * 512], ps[:, half, :], ACT.Identity,
                                   bias=bq[:, 1, u:u + 1], scale=ATT_SCALE).then_inc(bank_free[half], 1)

            write_hi(Unit(U_Q) + LEAD)
            act.wait_ge(bq_scaled, 1)
            query_out(0, uses.stage(BANK_01), 0)
            uses.stage(BANK_23)
            Kq = uses.stage({0: PAIRS - 1, 1: PAIRS - 1})
            uses.stage({0: TT, 1: TT})

            for s in range(STEPS + 4):
                u, n = divmod(s, TT)
                if s < STEPS:
                    if n == 0 and u + 1 < PAIRS:
                        write_hi(Unit(U_Q + u + 1) + LEAD)
                    if n == TT - 1 and u + 1 < PAIRS:
                        query_out(u + 1, Kq, u)
                    if n > 0:
                        act.wait_ge(scores_ready, s + 1)
                        if s >= 2:
                            act.wait_ge(probs_ready, s - 1)
                        act.activation(Sm[:, s % 2], ps[:, 2:4, 0:P], ACT.Copy).then_inc(prev_copied, 1)
                e = s - 1
                if 0 <= e < STEPS:
                    act.wait_ge(sinkarg_ready, e + 1)
                    for a in range(2):
                        act.activation(Pr[:, e % 2, a], Sm[:, e % 2, a], ACT.Exp, bias=st[:, e % 4, 1, a:a + 1],
                                       accum_out=st[:, e % 4, 3, a:a + 1])
                    act.activation(st[:, e % 4, 4], st[:, e % 4, 2], ACT.Exp).then_inc(probs_ready, 1)
                e = s - 4
                if 0 <= e < STEPS:
                    act.wait_ge(oT_ready, e + 1)
                    act.activation(yT[:, e // TT, (e % TT) * P:(e % TT + 1) * P], ps[:, 7, 0:P], ACT.Copy
                                   ).then_inc(oT_copied, 1)
                k = s - (STEPS - 2 * TT + 2)
                if 0 <= k < 6:
                    act.wait_ge(scores_ready, s)
                    act.wait_ge(oT_copied, (k + 1) * TT)
                    y_hi(k)
                if s in (STEPS - TT + 2, STEPS - TT + 4):
                    write_hi(Unit(U_BOUT + (s - (STEPS - TT)) // 2 - 1) + LEAD)
            act.wait_ge(oT_copied, STEPS)
            act.wait_ge(rcp_ready, STEPS)
            for k in (6, 7):
                y_hi(k)
            for j in (1, 2):
                write_hi(Unit(U_BOUT + 2 * j) + LEAD)
                write_hi(Unit(U_BOUT + 2 * j + 1) + LEAD)
                uses.stage(DOWN)
            down_and_norm(Unit(U_BOUT + 6), 3)
            ffn(1, 4)

        @block.vector
        def _(dve):
            uses = BankUses()

            def write_lo(u):
                if u.base >= UNITS:
                    return
                dve.wait_ge(hi_ready, u.n + 1)
                dve.tensor_tensor(wl[:, u.slot, :], raw[:, u.raw, :], wh[:, u.slot, :].bitcast(F32), ALU.subtract
                                  ).then_inc(lo_ready, 1)

            def mean_square(norm, t):
                dve.wait_ge(ssq_ready, norm * TT + t + 1)
                dve.tensor_scalar(ms[:, t:t + 1], ssq[:, t:t + 1], 1.0 / D, EPS, ALU.mult, ALU.add
                                  ).then_inc(ms_ready, 1)

            def x_normed(norm, t):
                dve.wait_ge(rstd_ready, norm * TT + t + 1)
                if norm == 4:
                    dve.wait_ge(gain_loaded, 16)
                    if t >= XS:
                        dve.wait_ge(out_stored[t % XS], 16 * (t // XS))
                    for piece, c in output_pieces:
                        if piece == t:
                            dve.scalar_tensor_tensor(xs[:, t % XS, c], X[:, t, c], rstd[:, t:t + 1],
                                                     gain_row[:, c], ALU.mult, ALU.mult).then_inc(xs_ready, 1)
                else:
                    dve.tensor_scalar(xs[:, t % XS, :], X[:, t, :], rstd[:, t:t + 1], None, ALU.mult
                                      ).then_inc(xs_ready, 1)

            def xt_lo(norm, K, t):
                for j in range(2):
                    b = 2 * (t % 2) + j
                    dve.wait_ge(xt_hi_ready, (norm * TT + t) * 2 + j + 1)
                    dve.tensor_tensor(xl[:, 4 * j:4 * j + 4, t * P:(t + 1) * P],
                                      ps[:, b, :].rearrange("p (k n) -> p k n", k=4),
                                      xh[:, 4 * j:4 * j + 4, t * P:(t + 1) * P].bitcast(F32), ALU.subtract
                                      ).then_inc(bank_free[b], 1)

            def add_tile(K, t):
                for half in range(2):
                    g = 2 * t + half
                    b = 4 + g % 4
                    dve.wait_ge(bank_full[b], K[b] + g // 4 + 1)
                    xv = X[:, t, half * 512:(half + 1) * 512]
                    dve.tensor_tensor(xv, ps[:, b, :], xv, ALU.add).then_inc(bank_free[b], 1)

            def down(pair, x_anew=False):
                K = uses.stage(DOWN)
                for t in range(TT):
                    if x_anew:
                        dve.wait_ge(x_loaded[t], 32)
                    add_tile(K, t)
                    if t in (1, 3):
                        write_lo(pair + (LEAD + t // 2))

            def down_and_norm(pair, norm, last=False):
                Kd = uses.stage(DOWN)
                Kn = None if last else uses.stage(NORM)
                for t in range(TT + 3):
                    if t < TT:
                        add_tile(Kd, t)
                    if 1 <= t <= TT:
                        x_normed(norm, t - 1)
                    if t in (1, 2):
                        write_lo(pair + (LEAD + t - 1))
                    if t >= 3 and not last:
                        xt_lo(norm, Kn, t - 3)
                    if t < TT:
                        mean_square(norm, t)

            K = uses.stage(NORM)
            for t in range(TT + 2):
                if t < TT:
                    mean_square(0, t)
                if t >= 2:
                    xt_lo(0, K, t - 2)
                if t < TT:
                    x_normed(0, t)
                if t == 5:
                    write_lo(Unit(U_GATES))
            for j in range(2):
                write_lo(Unit(U_HEADS + j))

            dve.wait_ge(bgate_loaded, 32)
            dve.tensor_scalar(bgate[0:NH_A, 1:2], bgate[0:NH_A, 0:1], 1.0 / GATE_CAP, None, ALU.mult)
            dve.tensor_scalar(bgate[32:32 + NH_A, 1:2], bgate[32:32 + NH_A, 0:1], 1.0 / GATE_CAP, None, ALU.mult
                              ).then_inc(gate_dve, 1)
            write_lo(Unit(U_HEADS + 2))
            K = uses.stage(BANK_45)
            dve.wait_ge(bank_free[5], K[5] + 1)
            dve.tensor_scalar(ig[:], ig[:], GATE_CAP, None, ALU.mult).then_inc(gate_dve, 1)
            dve.wait_ge(gate_act, 1)
            dve.tensor_scalar(one_enf[:], enf[:], 1.0, None, ALU.add).then_inc(gate_dve, 1)
            dve.wait_ge(gate_dve, 3)
            dve.scalar_tensor_tensor(enf[:], one_enf[:], -1.0, enf[:], ALU.add, ALU.subtract
                                     ).then_inc(gate_dve, 1)
            dve.wait_ge(gate_dve, 4)
            dve.wait_ge(gate_act, 3)
            dve.tensor_tensor(enf[:], enf[:], fg[:], ALU.mult).then_inc(gate_dve, 1)
            dve.wait_ge(gate_dve, 5)
            dve.tensor_tensor(lf[:], enf[:], lnu[:], ALU.subtract).then_inc(gate_dve, 1)
            dve.wait_ge(gate_dve, 6)
            dve.wait_ge(const_step, 11)
            dve.tensor_tensor_scan(brow[:], chunk_mask[:], lf[:], 0.0, ALU.mult, ALU.add
                                   ).then_inc(gate_dve, 1)
            dve.tensor_tensor_scan(mrow[:], lf[:], ig[:], 0.0, ALU.add, ALU.max
                                   ).then_inc(gate_dve, 1)
            dve.wait_ge(gate_dve, 8)
            dve.tensor_tensor(G[0:NH_A, :], ig[:], brow[:], ALU.subtract).then_inc(gate_dve, 1)
            dve.tensor_tensor(negm[:], brow[:], mrow[:], ALU.subtract).then_inc(gate_dve, 1)
            chunks = lambda r: r[:].rearrange("h (c t) -> h c t", t=P)
            dve.tensor_copy(mprev[:, 0, 1:TT], chunks(mrow)[:, 0:TT - 1, P - 1]).then_inc(gate_dve, 1)
            dve.wait_ge(gate_dve, 11)
            last_negm = chunks(negm)[:, :, P - 1:P]
            dve.tensor_tensor(mprev[:, 1, :], mprev[:, 0, :], last_negm.rearrange("h c o -> h (c o)"), ALU.add)
            dve.tensor_tensor(chunks(diff), chunks(negm), mprev[:, 0, :].unsqueeze(2).to_broadcast([NH_A, TT, P]),
                              ALU.add)
            dve.tensor_tensor(chunks(brow), chunks(G[0:NH_A]), last_negm.to_broadcast([NH_A, TT, P]), ALU.add
                              ).then_inc(gate_dve, 1)
            write_lo(Unit(U_HEADS + 3))

            def scale_head(h):
                dve.wait_ge(num_ready, h * TT + TT)
                dve.tensor_scalar(hsq[:, 1, :], hsq[:, 0, :], 1.0 / DV, EPS, ALU.mult, ALU.add
                                  ).then_inc(hms_ready, 1)
                dve.wait_ge(hrs_ready, h + 1)
                dve.tensor_tensor(H[:], H[:], hsq[:, 2, :].unsqueeze(2).to_broadcast([P, TT, DV]), ALU.mult
                                  ).then_inc(H_ready, 1)

            def gate_head(h):
                K = uses.stage(BANK_4567)
                for j in range(2):
                    for half in range(2):
                        b = 4 + 2 * j + half
                        dve.wait_ge(bank_full[b], K[b] + 1)
                        yv = yT[:, ds(2 * h + j, 1), half * 512:(half + 1) * 512].squeeze(1)
                        dve.scalar_tensor_tensor(yv, ps[:, b, :], hn[:, ds(2 * h + j, 1)], yv, ALU.mult, ALU.mult
                                                 ).then_inc(bank_free[b], 1)

            def head(h, turn, first):
                un = [Unit(U_HEADS + j, turn) for j in range(6)]
                write_lo(un[0] + LEAD)
                Kq = uses.stage(BANK_01)
                if not first:
                    scale_head(h - 1)
                    gate_head(h - 1)
                write_lo(un[1] + LEAD)
                uses.stage(BANK_23)
                write_lo(un[2] + LEAD)
                write_lo(un[3] + LEAD)
                uses.stage(BANK_4567)
                if first:
                    K = uses.stage(BANK_67)
                    for j in range(2):
                        dve.wait_ge(bank_full[6 + j], K[6 + j] + 1)
                        src = ps[:, 6 + j, :].rearrange("p (c g n) -> p c g n", c=4, g=4)[:, :, 0:3, 0:NH_A]
                        dve.tensor_copy(cols[:, 4 * j:4 * j + 4], src).then_inc(bank_free[6 + j], 1)
                    dve.wait_ge(bank_free[7], K[7] + 1)
                dve.wait_ge(ein_loaded, h * 16 + 16)
                dve.wait_ge(bank_free[1], Kq[1] + 1)
                dve.tensor_tensor(qe[:], qe[:], qT[:], ALU.mult).then_inc(qe_ready, 1)
                dve.wait_ge(neg_loaded, h * 16 + 16)
                dve.tensor_tensor(SwT[:], SwT[:], cols[:, :, 0, ds(h, 1)].to_broadcast([P, TT, P]), ALU.add
                                  ).then_inc(D_ready, 1)
                dve.wait_ge(D_ready, h + 1)
                dve.scalar_tensor_tensor(SwT[:], SwT[:], 0.0, mask_neg[:].unsqueeze(1).to_broadcast([P, TT, P]),
                                         ALU.min, ALU.add).then_inc(Dm_ready, 1)
                Ks = uses.stage(BANK_01)
                K = uses.stage(BANK_23)
                for j in range(2):
                    dve.wait_ge(bank_full[2 + j], K[2 + j] + 1)
                    dve.tensor_tensor(kw[:, 4 * j:4 * j + 4, :], ps[:, 2 + j, :].rearrange("p (c n) -> p c n", c=4),
                                      cols[:, 4 * j:4 * j + 4, 2, ds(h, 1)].to_broadcast([P, 4, P]), ALU.mult
                                      ).then_inc(bank_free[2 + j], 1)
                dve.wait_ge(E_ready, h + 1)
                for j in range(2):
                    dve.wait_ge(bank_full[j], Ks[j] + 1)
                    sv = SwT[:, 4 * j:4 * j + 4, :]
                    dve.tensor_tensor(sv, ps[:, j, :].rearrange("p (c n) -> p c n", c=4), sv, ALU.mult
                                      ).then_inc(bank_free[j], 1)
                uses.stage(BANK_4567)
                uses.stage(BANK_01)
                uses.stage(BANK_23)
                Ks = uses.stage(STATE)
                for c in range(TT):
                    if c % 4 == 0:
                        write_lo(un[4 + c // 4] + LEAD)
                    i = 2 * c
                    b = 4 + i % 4
                    dve.wait_ge(bank_full[b], Ks[b] + i // 4 + 1)
                    den = ps[:, b, DV:DV + 1]
                    dve.scalar_tensor_tensor(dn[:, c, 0:1], den, -1.0, cols[:, c, 1, ds(h, 1)], ALU.mult, ALU.max
                                             ).then_inc(den_step, 1)
                    dve.wait_ge(den_step, (h * TT + c) * 2 + 1)
                    dve.tensor_tensor(dn[:, c, 1:2], den, dn[:, c, 0:1], ALU.max).then_inc(den_step, 1)
                    dve.wait_ge(den_step, (h * TT + c) * 2 + 2)
                    dve.reciprocal(dn[:, c, 2:3], dn[:, c, 1:2]).then_inc(den_ready, 1)
                    if c < TT - 1:
                        i = 2 * c + 1
                        b = 4 + i % 4
                        dve.wait_ge(bank_full[b], Ks[b] + i // 4 + 1)
                        new = C[:, (c + 1) % 2, 0:W1]
                        if c == 0:
                            dve.tensor_copy(new, ps[:, b, 0:W1]).then_inc(bank_free[b], 1)
                        else:
                            dve.scalar_tensor_tensor(new, C[:, c % 2, 0:W1], decay[:, ds(h * TT + c, 1)],
                                                     ps[:, b, 0:W1], ALU.mult, ALU.add).then_inc(bank_free[b], 1)

            dve.wait_ge(decay_loaded, 16)
            dve.wait_ge(consts_loaded, 16 * 5)
            dve.tensor_scalar(sink[:, 1, :], sink[:, 0, :], -1.0, None, ALU.mult)
            dve.tensor_scalar(bq[:, 1, :], bq[:, 0, :], ATT_SCALE, None, ALU.mult).then_inc(bq_scaled, 1)
            head(0, 0, True)
            with dve.Fori(1, NH_A) as h:
                uses.enter_loop(h - 1, HEAD_USES)
                head(h, h, False)
            uses.leave_loop(NH_A - 1)

            scale_head(NH_A - 1)
            down(Unit(U_AOUT), x_anew=True)
            gate_head(NH_A - 1)
            down(Unit(U_AOUT + 2))
            down(Unit(U_AOUT + 4))
            down_and_norm(Unit(U_AOUT + 6), 1)

            def product(tile, j, b0=0):
                Kg = [uses.so_far(b0), uses.so_far(b0 + 1)]
                K = uses.stage(BANK_23)
                for half in range(2):
                    b = 2 + half
                    c = slice(half * 512, (half + 1) * 512)
                    dve.wait_ge(bank_free[b0 + half], Kg[half])
                    if not isinstance(tile, int) or tile:
                        dve.wait_ge(h_ready, 2 * tile)
                    dve.wait_ge(bank_full[b], K[b] + 1)
                    dve.tensor_tensor(hf[:, c], ps[:, b, :], sg[:, c], ALU.mult).then_inc(bank_free[b], 1)
                for half in range(2):
                    c = slice(half * 512, (half + 1) * 512)
                    dve.wait_ge(hh_ready, 2 * tile + half + 1)
                    dve.tensor_tensor(hl[:, j, c], hf[:, c], hh[:, j, c].bitcast(F32), ALU.subtract
                                      ).then_inc(h_ready, 1)

            def ffn(l, norm_after):
                u0, t0 = U_FFN[l], l * FT
                for j in range(2):
                    write_lo(Unit(u0 + 2 * j) + LEAD)
                    uses.stage(BANK_01 if j else BANK_45)
                    write_lo(Unit(u0 + 2 * j + 1) + LEAD)
                    product(t0 + j, j, 0 if j else 4)

                def pair(i, un):
                    write_lo(un + LEAD)
                    uses.stage(BANK_01)
                    down(un + 1)
                    write_lo(un + (3 + LEAD))
                    product(i * 2 + t0, 0)
                    write_lo(un + (4 + LEAD))
                    uses.stage(BANK_01)
                    write_lo(un + (5 + LEAD))
                    product(i * 2 + (t0 + 1), 1)

                with dve.Fori(1, FP - 1) as i:
                    uses.enter_loop(i - 1, FFN_USES)
                    pair(i, Unit(u0 + 4, i - 1))
                uses.leave_loop(FP - 2)
                pair(FP - 1, Unit(u0 + 4 + RING * (FP - 2)))
                down_and_norm(Unit(u0 + 3 * FT - 2), norm_after, last=(l == 1))

            ffn(0, 2)

            write_lo(Unit(U_KV) + LEAD)
            K = uses.stage(BANK_45)
            for half in range(2):
                b = 4 + half
                dve.wait_ge(bank_full[b], K[b] + 1)
                dve.tensor_scalar(kTb[:, half * 512:(half + 1) * 512], ps[:, b, :], bkv[:, 0:1], None, ALU.add
                                  ).then_inc(bank_free[b], 1)
            write_lo(Unit(U_KV + 1) + LEAD)
            K = uses.stage(BANK_23)
            for half in range(2):
                dve.wait_ge(bank_full[2 + half], K[2 + half] + 1)
                dve.tensor_scalar(vT[:, half * 512:(half + 1) * 512], ps[:, 2 + half, :], bkv[:, 1:2], None, ALU.add
                                  ).then_inc(bank_free[2 + half], 1)

            write_lo(Unit(U_Q) + LEAD)
            uses.stage(BANK_01)
            K = uses.stage(BANK_23)
            for j in range(2):
                dve.wait_ge(bank_full[2 + j], K[2 + j] + 1)
                dve.tensor_copy(vb[:, 4 * j:4 * j + 4, :], ps[:, 2 + j, :].rearrange("p (c n) -> p c n", c=4)
                                ).then_inc(bank_free[2 + j], 1)
            uses.stage({0: PAIRS - 1, 1: PAIRS - 1})
            Ko = uses.stage({0: TT, 1: TT})
            le = keep_le[:].bitcast(U32).unsqueeze(1).to_broadcast([P, 2, P])
            cur = keepT_cur[:].unsqueeze(1).to_broadcast([P, 2, P])
            prv = keepT_prev[:].unsqueeze(1).to_broadcast([P, 2, P])

            def add_output(t, half):
                if t == 0 and half == 0:
                    dve.wait_ge(bout_added, TT)
                dve.wait_ge(bank_full[half], Ko[half] + t + 1)
                xv = X[:, t, half * 512:(half + 1) * 512]
                dve.tensor_tensor(xv, ps[:, half, :], xv, ALU.add).then_inc(bank_free[half], 1)

            for s in range(STEPS + 3):
                u, n = divmod(s, TT)
                t = s - (STEPS - TT + 1)
                if 0 <= t < TT:
                    add_output(t, 1)
                    if t in (1, 3):
                        write_lo(Unit(U_BOUT + t // 2) + LEAD)
                if s < STEPS:
                    if n == 0 and u + 1 < PAIRS:
                        write_lo(Unit(U_Q + u + 1) + LEAD)
                    if n == 0:
                        if s >= 2:
                            dve.wait_ge(probs_ready, s - 1)
                        dve.memset(Sm[:, s % 2], NEG).then_inc(blank_set, 1)
                        dve.wait_ge(blank_set, u + 1)
                    else:
                        dve.wait_ge(prev_copied, (TT - 1) * u + n)
                    dve.wait_ge(scores_ready, s + 1)
                    dve.copy_predicated(Sm[:, s % 2], le, ps[:, 2:4, P:2 * P]).then_inc(merged, 1)
                    dve.wait_ge(merged, s + 1)
                    dve.tensor_reduce(st[:, s % 4, 0], Sm[:, s % 2], AX_X, ALU.max).then_inc(rowmax_ready, 1)
                    dve.wait_ge(rowmax_ready, s + 1)
                    dve.scalar_tensor_tensor(st[:, s % 4, 1], st[:, s % 4, 0], -1.0, sink[:, 1, u::PAIRS],
                                             ALU.mult, ALU.min).then_inc(negmax_ready, 1)
                    dve.wait_ge(negmax_ready, s + 1)
                    dve.tensor_tensor(st[:, s % 4, 2], st[:, s % 4, 1], sink[:, 0, u::PAIRS], ALU.add
                                      ).then_inc(sinkarg_ready, 1)
                    if u + 1 == PAIRS:
                        add_output(n, 0)
                e = s - 3
                if 0 <= e < STEPS:
                    dve.wait_ge(o_ready, e + 1)
                    dve.tensor_tensor(on[:].rearrange("p (a d) -> p a d", a=2),
                                      ps[:, 6, 0:P].rearrange("p (a d) -> p a d", a=2),
                                      st[:, e % 4, 5].unsqueeze(2).to_broadcast([P, 2, DH_B]), ALU.mult
                                      ).then_inc(on_ready, 1)
                e = s - 2
                if 0 <= e < STEPS:
                    b = 4 + e % 2
                    dve.wait_ge(probsT_ready, e + 1)
                    pT = ps[:, b, 0:2 * P].rearrange("p (a n) -> p a n", a=2)
                    dve.tensor_tensor(PTc[:], pT, cur, ALU.mult).then_inc(pt_ready, 1)
                    dve.tensor_tensor(PTp[:], pT, prv, ALU.mult).then_inc(pt_ready, 1)
                e = s - 1
                if 0 <= e < STEPS:
                    dve.wait_ge(probs_ready, e + 1)
                    dve.tensor_tensor(st[:, e % 4, 0], st[:, e % 4, 3], st[:, e % 4, 4], ALU.add
                                      ).then_inc(den_sum, 1)
                    dve.wait_ge(den_sum, e + 1)
                    dve.reciprocal(st[:, e % 4, 5], st[:, e % 4, 0]).then_inc(rcp_ready, 1)
            for j in (1, 2):
                down(Unit(U_BOUT + 2 * j))
            down_and_norm(Unit(U_BOUT + 6), 3)
            ffn(1, 4)

        @block.tensor
        def _(pe):
            uses = BankUses()
            mm = nc.tensor.matmul
            after_pair = [False]

            def begin(first_matmul):
                first_matmul.then_inc(unit_begun, 2 if after_pair[0] else 1)
                after_pair[0] = False

            def three_passes(b, halves, ah, al, bh, bl, start, stop):
                c = [slice(half * 512, (half + 1) * 512) for half in range(2)]
                ms_ = [mm(ps[:, b + half, :], ah, t[:, c[half]], start=start and t is bh, stop=False)
                       for half in halves for t in (bh, bl)]
                ms_ += [mm(ps[:, b + half, :], al, bh[:, c[half]], start=False, stop=stop) for half in halves]
                if stop:
                    for half, m in zip(halves, ms_[-len(halves):]):
                        m.then_inc(bank_full[b + half], 1)
                return ms_[0]

            def columns(u, b0, K, between=None):
                pe.wait_ge(lo_ready, u.n + 1)
                for half in range(2):
                    pe.wait_ge(bank_free[b0 + half], K[b0 + half])
                for k in range(KT):
                    column_step(u, b0, (0, 1), k)
                    if between is not None and k % 2 == 0:
                        between(k // 2)

            def column_step(u, b0, halves, k):
                w = slice(k * P, (k + 1) * P)
                m0 = three_passes(b0, halves, wh[:, u.slot, w], wl[:, u.slot, w],
                                  xh[:, k, :], xl[:, k, :], k == 0, k == KT - 1)
                if k == 0 and halves[0] == 0:
                    begin(m0)

            def down(u, lhs, lhs_ready, K, after_tile=None):
                for t, j in [(0, 0), (1, 0), (0, 1), (1, 1)] + [(t, j) for t in range(2, TT) for j in range(2)]:
                    b = 4 + 2 * (t % 2)
                    if j == 0:
                        for half in range(2):
                            pe.wait_ge(bank_free[b + half], K[b + half] + t // 2)
                    if t == 0:
                        pe.wait_ge(lo_ready, u.n + j + 1)
                    if t in (0, TT // 2):
                        lhs_ready(j, t // (TT // 2))
                    ah, al = lhs(j)
                    s = (u + j).slot
                    tok = slice(t * P, (t + 1) * P)
                    for halves in ([(0,), (1,)] if j == 1 and t in (0, TT - 1) else [(0, 1)]):
                        m0 = three_passes(b, halves, ah[:, tok], al[:, tok], wh[:, s, :], wl[:, s, :], j == 0, j == 1)
                    if t == 0 and j == 0:
                        begin(m0)
                    if j == 1 and after_tile is not None:
                        after_tile(t)
                after_pair[0] = True

            def x_transposes(norm, K, t):
                pe.wait_ge(xs_ready, norm * TT + t + 1)
                for j in range(2):
                    b = 2 * (t % 2) + j
                    if norm or t >= 2:
                        pe.wait_ge(bank_free[b], K[b] + t // 2)
                    for k in range(4):
                        f = (4 * j + k) * P
                        m = nc.tensor.transpose(ps[:, b, k * P:(k + 1) * P], xs[:, t % XS, f:f + P], ident[:])
                    m.then_inc(bank_full[b], 1)

            def end_of_norm(norm, Kn, u):
                K = uses.stage(BANK_45)
                for half in range(2):
                    if half == 0:
                        pe.wait_ge(lo_ready, u.n + 1)
                    if norm:
                        pe.wait_ge(bank_free[4 + half], K[4 + half])
                    for k in range(KT):
                        if k % 4 == 0:
                            b = 2 + k // 4
                            pe.wait_ge(bank_free[b], Kn[b] + 2 * half + 2)
                        column_step(u, 4, (half,), k)
                        if half == 0 and k in (1, 4):
                            x_transposes(norm, Kn, TT - 2 + k // 4)

            def down_and_norm(u, lhs, lhs_ready, norm):
                Kd = uses.stage(DOWN)
                Kn = uses.stage(NORM)
                down(u, lhs, lhs_ready, Kd, lambda t: x_transposes(norm, Kn, t - 2) if t >= 2 else None)
                end_of_norm(norm, Kn, u + 2)

            pe.wait_ge(consts_set, 5)
            K = uses.stage(NORM)
            for t in range(TT - 2):
                x_transposes(0, K, t)
            end_of_norm(0, K, Unit(U_GATES))

            def head_transposes(h):
                K = uses.stage(BANK_4567)
                pe.wait_ge(H_ready, h + 1)
                for j in range(2):
                    for half in range(2):
                        b = 4 + 2 * j + half
                        pe.wait_ge(bank_free[b], K[b])
                        for c in range(4):
                            m = nc.tensor.transpose(ps[:, b, c * P:(c + 1) * P],
                                                    H[:, 4 * half + c, j * P:(j + 1) * P], ident[:])
                        m.then_inc(bank_full[b], 1)

            def head(h, turn, first):
                un = [Unit(U_HEADS + j, turn) for j in range(6)]
                K0 = uses.stage(BANK_01)
                columns(un[0], 0, K0)
                if not first:
                    head_transposes(h - 1)
                K2 = uses.stage(BANK_23)
                columns(un[1], 2, K2)

                def v_tiles(t0):
                    K = uses.stage(BANK_4567)
                    pe.wait_ge(lo_ready, un[3].n + 1)
                    for t in range(t0, t0 + 4):
                        b = 4 + t % 4
                        if t0 or not first or b < 6:
                            pe.wait_ge(bank_free[b], K[b])
                        for k in range(KT):
                            xv = slice(t * P, (t + 1) * P)
                            s = un[2].slot
                            rh = wh[:, s:s + 2, k * P:(k + 1) * P]
                            rl = wl[:, s:s + 2, k * P:(k + 1) * P]
                            dst = ps[:, b, 0:DV]
                            m0 = mm(dst, xh[:, k, xv], rh, start=k == 0, stop=False)
                            if t == 0 and k == 0:
                                begin(m0)
                            mm(dst, xh[:, k, xv], rl, start=False, stop=False)
                            m = mm(dst, xl[:, k, xv], rh, start=False, stop=k == KT - 1)
                        m.then_inc(bank_full[b], 1)

                v_tiles(0)
                K = uses.stage(BANK_01)
                pe.wait_ge(bank_free[1], K[1])
                pe.wait_ge(bank_free[3], K2[3] + 1)
                for c in range(TT):
                    t = slice(c * P, (c + 1) * P)
                    m = mm(ps[:, c // 4, (c % 4) * P:(c % 4 + 1) * P], kT[:, t], qT[:, t], start=True, stop=True)
                    if c % 4 == 3:
                        m.then_inc(bank_full[c // 4], 1)
                K = uses.stage(BANK_23)
                for c in range(TT):
                    b = 2 + c // 4
                    m = nc.tensor.transpose(ps[:, b, (c % 4) * P:(c % 4 + 1) * P], kT[:, c * P:(c + 1) * P], ident[:])
                    if c % 4 == 3:
                        m.then_inc(bank_full[b], 1)
                if first:
                    K = uses.stage(BANK_67)
                    pe.wait_ge(gate_act, 5)
                    for j in range(2):
                        pe.wait_ge(bank_free[6 + j], K[6 + j])
                        for c in range(4):
                            t = 4 * j + c
                            m = nc.tensor.transpose(ps[:, 6 + j, c * P:(c + 1) * P], G[:, t * P:(t + 1) * P], ident[:])
                        m.then_inc(bank_full[6 + j], 1)
                v_tiles(4)
                Ko = [uses.stage(BANK_01), uses.stage(BANK_23)]
                Ks = uses.stage(STATE)
                after_pair[0] = True

                def chunk(c):
                    if c == 0:
                        pe.wait_ge(bank_free[1], Ko[0][1])
                        pe.wait_ge(qe_ready, h + 1)
                        pe.wait_ge(bank_free[3], Ko[1][3])
                        for b in range(4, 8):
                            pe.wait_ge(bank_free[b], Ks[b])
                    i = 2 * c
                    b = 4 + i % 4
                    pe.wait_ge(bank_free[b], Ks[b] + i // 4)
                    dst = ps[:, b, 0:W1]
                    m = mm(dst, SwT[:, c, :], v1[:, c, :], start=True, stop=c == 0)
                    if c:
                        bu = 4 + (2 * c - 1) % 4
                        pe.wait_ge(bank_free[bu], Ks[bu] + (2 * c - 1) // 4 + 1)
                        m = mm(dst, qe[:, c * P:(c + 1) * P], C[:, c % 2, 0:W1], start=False, stop=True)
                    m.then_inc(bank_full[b], 1)
                    if c < TT - 1:
                        i = 2 * c + 1
                        b = 4 + i % 4
                        pe.wait_ge(bank_free[b], Ks[b] + i // 4)
                        mm(ps[:, b, 0:W1], kw[:, c, :], v1[:, c, :], start=True, stop=True
                           ).then_inc(bank_full[b], 1)

                columns(un[4], 0, Ko[0], between=lambda i: chunk(i))
                columns(un[5], 2, Ko[1], between=lambda i: chunk(4 + i))

            head(0, 0, True)
            with pe.Fori(1, NH_A) as h:
                uses.enter_loop(h - 1, HEAD_USES)
                head(h, h, False)
            uses.leave_loop(NH_A - 1)

            def y_tiles(k0):
                return lambda j: (xh[:, k0 + j, :], xl[:, k0 + j, :])

            def h_tiles(j):
                return hh[:, j, :], hl[:, j, :]

            def y_tiles_ready(k0):
                return lambda j, half: pe.wait_ge(y_ready, k0 + j + 1)

            def h_tiles_ready(first_tile):
                return lambda j, half: pe.wait_ge(h_ready, (first_tile + j) * 2 + half + 1)

            for j in range(3):
                down(Unit(U_AOUT + 2 * j), y_tiles(2 * j), y_tiles_ready(2 * j), uses.stage(DOWN))
                if j == 0:
                    head_transposes(NH_A - 1)
            down_and_norm(Unit(U_AOUT + 6), h_tiles, y_tiles_ready(6), 1)

            def ffn(l, norm_after):
                u0, t0 = U_FFN[l], l * FT
                columns(Unit(u0 + 1), 2, uses.stage(BANK_23))
                columns(Unit(u0 + 2), 0, uses.stage(BANK_01))
                columns(Unit(u0 + 3), 2, uses.stage(BANK_23))
                with pe.Fori(1, FP) as i:
                    t = i - 1
                    uses.enter_loop(t, FFN_USES)
                    columns(Unit(u0 + 4, t), 0, uses.stage(BANK_01))
                    down(Unit(u0 + 5, t), h_tiles, h_tiles_ready(t * 2 + t0), uses.stage(DOWN))
                    columns(Unit(u0 + 7, t), 2, uses.stage(BANK_23))
                    columns(Unit(u0 + 8, t), 0, uses.stage(BANK_01))
                    columns(Unit(u0 + 9, t), 2, uses.stage(BANK_23))
                uses.leave_loop(FP - 1)
                last = (Unit(u0 + 3 * FT - 2), h_tiles, h_tiles_ready(t0 + FT - 2))
                if l == 0:
                    down_and_norm(*last, norm_after)
                else:
                    down(*last, uses.stage(DOWN))

            ffn(0, 2)

            K2 = uses.stage(BANK_23)
            columns(Unit(U_KV + 1), 2, K2)
            columns(Unit(U_Q), 0, uses.stage(BANK_01))
            K = uses.stage(BANK_23)
            pe.wait_ge(bank_free[3], K[3])
            for c in range(TT):
                b = 2 + c // 4
                m = nc.tensor.transpose(ps[:, b, (c % 4) * P:(c % 4 + 1) * P], vT[:, c * P:(c + 1) * P], ident[:])
                if c % 4 == 3:
                    m.then_inc(bank_full[b], 1)
            Kq = uses.stage({0: PAIRS - 1, 1: PAIRS - 1})
            Ko = uses.stage({0: TT, 1: TT})
            for b in range(2, 8):
                pe.wait_ge(bank_free[b], uses.before[b])

            def first_output_pair(t, half):
                un = Unit(U_BOUT)
                if t == 0 and half == 0:
                    pe.wait_ge(lo_ready, un.n + 2)
                    pe.wait_ge(y_ready, KT + 2)
                pe.wait_ge(bank_free[half], Ko[half] + t)
                for j in range(2):
                    tok = slice(t * P, (t + 1) * P)
                    m0 = three_passes(0, (half,), xh[:, j, tok], xl[:, j, tok], wh[:, (un + j).slot, :],
                                      wl[:, (un + j).slot, :], j == 0, j == 1)
                    if t == 0 and half == 0 and j == 0:
                        begin(m0)

            for s in range(STEPS + 4):
                u, n = divmod(s, TT)
                if s < STEPS:
                    if n == 0:
                        pe.wait_ge(bank_free[1], Kq[1] + u)
                    if s:
                        pe.wait_ge(merged, s)
                    c0 = 0 if n else P
                    for a in range(2):
                        r = slice(a * DH_B, (a + 1) * DH_B)
                        m = mm(ps[:, 2 + a, c0:2 * P], yT[r, u, n * P:(n + 1) * P],
                               kTb[r, (n - 1) * P + c0:(n + 1) * P], start=True, stop=True)
                    m.then_inc(scores_ready, 1)
                    if u + 1 < PAIRS and n < TT - 1:
                        un = Unit(U_Q + u + 1)
                        if n == 0:
                            pe.wait_ge(lo_ready, un.n + 1)
                            for half in range(2):
                                pe.wait_ge(bank_free[half], Kq[half] + u)
                        for k in ((0, 1) if n == 0 else (n + 1,)):
                            column_step(un, 0, (0, 1), k)
                    if u + 1 == PAIRS:
                        first_output_pair(n, 0)
                e = s - 2
                if 0 <= e < STEPS:
                    b = 4 + e % 2
                    pe.wait_ge(probs_ready, e + 1)
                    if e >= 2:
                        pe.wait_ge(pt_ready, 2 * (e - 1))
                    for a in range(2):
                        m = nc.tensor.transpose(ps[:, b, a * P:(a + 1) * P], Pr[:, e % 2, a], ident[:])
                    m.then_inc(probsT_ready, 1)
                e = s - 4
                if 0 <= e < STEPS:
                    pe.wait_ge(on_ready, e + 1)
                    if e >= 1:
                        pe.wait_ge(oT_copied, e)
                    nc.tensor.transpose(ps[:, 7, 0:P], on[:], ident[:]).then_inc(oT_ready, 1)
                e = s - 3
                if 0 <= e < STEPS:
                    ne = e % TT
                    pe.wait_ge(pt_ready, 2 * (e + 1))
                    if e >= 1:
                        pe.wait_ge(on_ready, e)
                    for a in range(2):
                        d = slice(a * DH_B, (a + 1) * DH_B)
                        m = mm(ps[:, 6, d], PTc[:, a], vb[:, ne, d], start=True, stop=ne == 0)
                        if ne:
                            m = mm(ps[:, 6, d], PTp[:, a], vb[:, ne - 1, d], start=False, stop=True)
                    m.then_inc(o_ready, 1)
                if u + 1 == PAIRS:
                    first_output_pair(n, 1)
            pe.wait_ge(oT_copied, STEPS)

            after_pair[0] = True
            for j in (1, 2):
                down(Unit(U_BOUT + 2 * j), y_tiles(2 * j), y_tiles_ready(KT + 2 * j), uses.stage(DOWN))
            down_and_norm(Unit(U_BOUT + 6), h_tiles, y_tiles_ready(KT + 6), 3)
            ffn(1, 4)


_INS = ['x', 'a_norm', 'a_w_in', 'a_b_gates', 'a_head_norm', 'a_w_out', 'kv_norm', 'w_kv', 'b_kv', 'b_norm',
        'b_w_q', 'b_b_q', 'b_sinks', 'b_w_out', 'b_b_out', 'ffn_norm', 'w_gate_up', 'w_down', 'final_norm']


def kernel(**inputs):
    import numpy as _np
    import concourse.bacc as _bacc
    from concourse import mybir as _mybir
    from concourse.bass_utils import run_bass_kernel_spmd as _run

    nc = _bacc.Bacc("TRN2", target_bir_lowering=False, num_devices=1)
    arrays, args = {}, []
    for name in _INS:
        a = _np.ascontiguousarray(inputs[name])
        arrays[f"in_{name}_dram"] = a
        args.append(nc.dram_tensor(f"in_{name}_dram", a.shape, _mybir.dt.from_np(a.dtype), kind="ExternalInput").ap())
    shape = inputs["x"].shape
    out = nc.dram_tensor("out_0_dram", shape, _mybir.dt.float32, kind="ExternalOutput").ap()
    yoco_kernel(nc, *args, out)
    r = _run(nc, [arrays], core_ids=[0])
    return r.results[0]["out_0_dram"]
```
